# Optimizing a Trainium2 kernel written in Bass

```python
import jax, jax.numpy as jnp
from jax import lax
import numpy as np

D_MODEL = 2048
BATCH = 1
SEQ = 256
DEPTH = 2
DEC_BATCH = 8
DEC_SEQ = 4
PAST_LEN = 1024
PAGE_SIZE = 128

D_A = D_MODEL // 2
A_GROUPS = 8
A_CHUNK = 128
B_HEADS = 8
B_HEAD_DIM = (D_MODEL // 2) // B_HEADS
D_B = B_HEADS * B_HEAD_DIM
MOBA_BLOCK = 256
MOBA_TOPK = 3
Q_BLOCK = 128
D_C = D_MODEL
CONV_W = 31
N_AB = (DEPTH + 1) // 2
N_CONV = DEPTH // 2
EPS = 1e-6
NEG = -1e30

kernel_name = 'hybrid_chunkmlp_moba_conformer_decode_step'

def rmsnorm(x, g):
    xf = x.astype(jnp.float32)
    r = lax.rsqrt(jnp.mean(xf * xf, axis=-1, keepdims=True) + EPS)
    return (xf * r).astype(x.dtype) * g

def layernorm(x, g, b):
    xf = x.astype(jnp.float32)
    mu = jnp.mean(xf, axis=-1, keepdims=True)
    var = jnp.mean(jnp.square(xf - mu), axis=-1, keepdims=True)
    return ((xf - mu) * lax.rsqrt(var + EPS)).astype(x.dtype) * g + b

def adaln_mod(c, w, b):
    m = jax.nn.silu(c) @ w + b
    return jnp.split(m[:, None, :], 3, axis=-1)

def alibi_slopes():
    return jnp.asarray(np.array([2.0 ** (-8.0 * (h + 1) / B_HEADS) for h in range(B_HEADS)], np.float32))

def chunk_mix(u, v, ws, bs):
    bn, L, _ = u.shape
    n = min(L, A_CHUNK)
    nc = L // n
    w = ws[:, :n, :n] * jnp.tril(jnp.ones((n, n), ws.dtype))
    vr = v.reshape(bn, nc, n, A_GROUPS, D_A // A_GROUPS)
    mix = jnp.einsum('gts,bcsgd->bctgd', w, vr) + bs[:, :n].T[None, None, :, :, None]
    return u * mix.reshape(bn, L, D_A)

def moba_attend(q, kb, vb, t, slopes):
    H, NB = kb.shape[0], kb.shape[1]
    qf = q * (B_HEAD_DIM ** -0.5)
    kbar = jnp.mean(kb.astype(jnp.float32), axis=2)
    j = t // MOBA_BLOCK
    g = jnp.einsum('hqd,hnd->hqn', qf.astype(jnp.float32), kbar)
    past = jnp.arange(NB)[None, None, :] < j[None, :, None]
    g = jnp.where(past, g, NEG)
    _, top = lax.top_k(g, min(MOBA_TOPK, NB))
    top_valid = top < j[None, :, None]
    own = jnp.broadcast_to(j[None, :, None], (H, q.shape[1], 1)).astype(top.dtype)
    sel = jnp.concatenate([top, own], axis=-1)
    valid = jnp.concatenate([top_valid, jnp.ones(own.shape, bool)], axis=-1)
    hidx = jnp.arange(H)[:, None, None]
    ks = kb[hidx, sel]
    vs = vb[hidx, sel]
    pos = sel[..., None] * MOBA_BLOCK + jnp.arange(MOBA_BLOCK)
    dist = (t[None, :, None, None] - pos).astype(jnp.float32)
    s = jnp.einsum('hqd,hqnkd->hqnk', qf, ks).astype(jnp.float32) - slopes[:, None, None, None] * dist
    s = jnp.where(valid[..., None] & (dist >= 0), s, NEG)
    p = jax.nn.softmax(s.reshape(H, q.shape[1], -1), axis=-1).reshape(s.shape)
    return jnp.einsum('hqnk,hqnkd->hqd', p.astype(vs.dtype), vs)

def pad_to_block(x, axis):
    L = x.shape[axis]
    Lp = -(-L // MOBA_BLOCK) * MOBA_BLOCK
    pads = [(0, 0)] * x.ndim
    pads[axis] = (0, Lp - L)
    return jnp.pad(x, pads)

def moba_prompt(q, k, v, slopes):
    bn, S = q.shape[0], q.shape[1]
    kp, vp = pad_to_block(k, 1), pad_to_block(v, 1)
    nb = kp.shape[1] // MOBA_BLOCK
    kb = kp.reshape(bn, nb, MOBA_BLOCK, B_HEADS, B_HEAD_DIM).transpose(0, 3, 1, 2, 4)
    vb = vp.reshape(bn, nb, MOBA_BLOCK, B_HEADS, B_HEAD_DIM).transpose(0, 3, 1, 2, 4)
    nq = S // Q_BLOCK
    qb = q.reshape(bn, nq, Q_BLOCK, B_HEADS, B_HEAD_DIM).transpose(0, 1, 3, 2, 4)
    tq = jnp.arange(S, dtype=jnp.int32).reshape(nq, Q_BLOCK)

    def per_seq(args):
        qs, kbs, vbs = args
        return lax.map(lambda a: moba_attend(a[0], kbs, vbs, a[1], slopes), (qs, tq))

    out = lax.map(per_seq, (qb, kb, vb))
    return out.transpose(0, 1, 3, 2, 4).reshape(bn, S, D_B)

def moba_sample(q, k, v, cache_k, cache_v, page_table, slopes):
    db, ds = q.shape[0], q.shape[1]
    past = page_table.shape[1] * cache_k.shape[1]
    tq = past + jnp.arange(ds, dtype=jnp.int32)

    def per_seq(args):
        qs, kn, vn, pt = args
        kall = pad_to_block(jnp.concatenate([cache_k[pt].reshape(past, B_HEADS, B_HEAD_DIM), kn], axis=0), 0)
        vall = pad_to_block(jnp.concatenate([cache_v[pt].reshape(past, B_HEADS, B_HEAD_DIM), vn], axis=0), 0)
        nb = kall.shape[0] // MOBA_BLOCK
        kb = kall.reshape(nb, MOBA_BLOCK, B_HEADS, B_HEAD_DIM).transpose(2, 0, 1, 3)
        vb = vall.reshape(nb, MOBA_BLOCK, B_HEADS, B_HEAD_DIM).transpose(2, 0, 1, 3)
        return moba_attend(qs.transpose(1, 0, 2), kb, vb, tq, slopes)

    out = lax.map(per_seq, (q, k, v, page_table))
    return out.transpose(0, 2, 1, 3).reshape(db, ds, D_B)

def ab_project(h, w_in, ln_g, ln_b, ws, bs):
    widths = [D_A, D_A, D_A, D_B, D_B, D_B, D_B]
    idx = [int(i) for i in np.cumsum(widths)[:-1]]
    u_a, v_a, z_a, q_b, k_b, v_b, z_b = jnp.split(h @ w_in, idx, axis=-1)
    bn, L = h.shape[0], h.shape[1]
    vn = layernorm(jax.nn.gelu(v_a), ln_g, ln_b)
    y_a = chunk_mix(jax.nn.gelu(u_a), vn, ws, bs) * jax.nn.silu(z_a)
    shp = (bn, L, B_HEADS, B_HEAD_DIM)
    return y_a, q_b.reshape(shp), k_b.reshape(shp), v_b.reshape(shp), z_b, vn

def conv_mixer(h, w_in, conv_w, conv_b, ln_g, ln_b, w_out, prev):
    a, b, z = jnp.split(h @ w_in, 3, axis=-1)
    glu = a * jax.nn.sigmoid(b)
    full = jnp.concatenate([prev.astype(glu.dtype), glu], axis=1)
    y = lax.conv_general_dilated(full, conv_w[:, None, :].astype(full.dtype), window_strides=(1,), padding='VALID',
                                 dimension_numbers=('NWC', 'WIO', 'NWC'), feature_group_count=D_C) + conv_b
    y = jax.nn.silu(layernorm(y, ln_g, ln_b)) * jax.nn.silu(z)
    return y @ w_out, full[:, -(CONV_W - 1):]

def setup_inputs(seed: int = 0) -> dict:
    key = jax.random.key(seed)
    ks = jax.random.split(key, 32)
    f = jnp.float32
    n_pages = PAST_LEN // PAGE_SIZE
    n_phys = (DEC_BATCH * n_pages * 5) // 4
    nrm = lambda k, s, sc: jax.random.normal(k, s, f) * sc
    d_ab_in = 3 * D_A + 4 * D_B
    perm = jax.random.permutation(ks[5], n_phys)[:DEC_BATCH * n_pages]
    return {
        'x_prompt': nrm(ks[0], (BATCH, SEQ, D_MODEL), 1.0),
        'x_sample': nrm(ks[1], (DEC_BATCH, DEC_SEQ, D_MODEL), 1.0),
        'cache_b_k': nrm(ks[2], (N_AB, n_phys, PAGE_SIZE, B_HEADS, B_HEAD_DIM), 1.0),
        'cache_b_v': nrm(ks[3], (N_AB, n_phys, PAGE_SIZE, B_HEADS, B_HEAD_DIM), 1.0),
        'state_c_conv': nrm(ks[4], (N_CONV, DEC_BATCH, CONV_W - 1, D_C), 0.5),
        'page_table': perm.reshape(DEC_BATCH, n_pages).astype(jnp.int32),
        'c_prompt': nrm(ks[6], (BATCH, D_MODEL), 1.0),
        'c_sample': nrm(ks[7], (DEC_BATCH, D_MODEL), 1.0),
        'ada_w': nrm(ks[8], (DEPTH, D_MODEL, 3 * D_MODEL), 0.5 * D_MODEL ** -0.5),
        'ada_b': nrm(ks[9], (DEPTH, 3 * D_MODEL), 0.01),
        'norm_g': 1.0 + nrm(ks[10], (DEPTH, D_MODEL), 0.05),
        'ab_w_in': nrm(ks[11], (N_AB, D_MODEL, d_ab_in), D_MODEL ** -0.5),
        'a_ln_g': 1.0 + nrm(ks[12], (N_AB, D_A), 0.05),
        'a_ln_b': nrm(ks[13], (N_AB, D_A), 0.05),
        'a_ws': nrm(ks[14], (N_AB, A_GROUPS, A_CHUNK, A_CHUNK), A_CHUNK ** -0.5),
        'a_bs': 1.0 + nrm(ks[15], (N_AB, A_GROUPS, A_CHUNK), 0.1),
        'ab_w_out': nrm(ks[16], (N_AB, D_A + D_B, D_MODEL), (D_A + D_B) ** -0.5),
        'c_w_in': nrm(ks[17], (N_CONV, D_MODEL, 3 * D_C), D_MODEL ** -0.5),
        'c_conv_w': nrm(ks[18], (N_CONV, CONV_W, D_C), CONV_W ** -0.5),
        'c_conv_b': nrm(ks[19], (N_CONV, D_C), 0.01),
        'c_ln_g': 1.0 + nrm(ks[20], (N_CONV, D_C), 0.05),
        'c_ln_b': nrm(ks[21], (N_CONV, D_C), 0.05),
        'c_w_out': nrm(ks[22], (N_CONV, D_C, D_MODEL), D_C ** -0.5),
        'final_norm_g': 1.0 + nrm(ks[23], (D_MODEL,), 0.05),
    }

def reference(x_prompt, x_sample, cache_b_k, cache_b_v, state_c_conv, page_table, c_prompt, c_sample,
              ada_w, ada_b, norm_g, ab_w_in, a_ln_g, a_ln_b, a_ws, a_bs, ab_w_out,
              c_w_in, c_conv_w, c_conv_b, c_ln_g, c_ln_b, c_w_out, final_norm_g):
    slopes = alibi_slopes()
    xp, xs = x_prompt, x_sample
    k_p, v_p, k_s, v_s, av_s, cv_p, cv_s = [], [], [], [], [], [], []
    for layer in range(DEPTH):
        shp, scp, gtp = adaln_mod(c_prompt, ada_w[layer], ada_b[layer])
        shs, scs, gts = adaln_mod(c_sample, ada_w[layer], ada_b[layer])
        hp = rmsnorm(xp, norm_g[layer]) * (1.0 + scp) + shp
        hs = rmsnorm(xs, norm_g[layer]) * (1.0 + scs) + shs
        i = layer // 2
        if layer % 2 == 0:
            ya_p, qp, kp, vp, zp, _ = ab_project(hp, ab_w_in[i], a_ln_g[i], a_ln_b[i], a_ws[i], a_bs[i])
            ya_s, qs, kn, vn, zs, vas = ab_project(hs, ab_w_in[i], a_ln_g[i], a_ln_b[i], a_ws[i], a_bs[i])
            yb_p = moba_prompt(qp, kp, vp, slopes) * jax.nn.silu(zp)
            yb_s = moba_sample(qs, kn, vn, cache_b_k[i], cache_b_v[i], page_table, slopes) * jax.nn.silu(zs)
            yp = jnp.concatenate([ya_p, yb_p], axis=-1) @ ab_w_out[i]
            ys = jnp.concatenate([ya_s, yb_s], axis=-1) @ ab_w_out[i]
            k_p.append(kp); v_p.append(vp); k_s.append(kn); v_s.append(vn); av_s.append(vas)
        else:
            zero_prev = jnp.zeros((xp.shape[0], CONV_W - 1, D_C), hp.dtype)
            yp, sp = conv_mixer(hp, c_w_in[i], c_conv_w[i], c_conv_b[i], c_ln_g[i], c_ln_b[i], c_w_out[i], zero_prev)
            ys, ss = conv_mixer(hs, c_w_in[i], c_conv_w[i], c_conv_b[i], c_ln_g[i], c_ln_b[i], c_w_out[i], state_c_conv[i])
            cv_p.append(sp); cv_s.append(ss)
        xp = xp + gtp * yp
        xs = xs + gts * ys
    y_prompt = rmsnorm(xp, final_norm_g)
    y_sample = rmsnorm(xs, final_norm_g)
    return (y_prompt, y_sample, jnp.stack(k_p), jnp.stack(v_p), jnp.stack(k_s), jnp.stack(v_s),
            jnp.stack(av_s), jnp.stack(cv_p), jnp.stack(cv_s))


_drawn_inputs = setup_inputs


def setup_inputs(seed=0):
    import zlib

    import numpy as np

    out = dict(_drawn_inputs(seed))
    spreads = {}
    factors = {'ada_b': 3.653, 'a_bs': 5.728, 'c_conv_b': 8.0, 'c_ln_g': 8.0, 'c_ln_b': 8.0}
    for name, (base, spread) in spreads.items():
        noise = np.random.default_rng([zlib.crc32(name.encode()), seed]).standard_normal(out[name].shape)
        drawn = base * np.exp(spread * noise) if base else spread * noise
        out[name] = __import__('jax').numpy.asarray(drawn.astype(out[name].dtype))
    for name, factor in factors.items():
        out[name] = (out[name] * factor).astype(out[name].dtype)
    return out
```

```python
from contextlib import ExitStack

import concourse.bass as bass
from concourse import mybir

F32 = mybir.dt.float32
F32R = mybir.dt.float32r
I32 = mybir.dt.int32
ACT = mybir.ActivationFunctionType
ALU = mybir.AluOpType
AX = mybir.AxisListType

P = 128
D = 2048
KC = D // P
SEQ = 256
NS, DS = 8, 4
SR0 = SEQ
R = SEQ + NS * DS
HEADS, HD = 8, 128
DA = 1024
GC = DA // P
PAGE, NPAGE = 128, 8
BLOCK = 256
NBLK = PAGE * NPAGE // BLOCK
PAST = PAGE * NPAGE
CW = 31
HALO = CW - 1
NC9 = 1 + NS
EPS = 1e-6
NEG = -1e30
QSCALE = HD ** -0.5
SLOPES = [2.0 ** (-8.0 * (h + 1) / HEADS) for h in range(HEADS)]

PAIRS_QKV, PAIRS_REST, PAIRS_OUT, PAIRS_AB, PAIRS_Z = 12, 16, 8, 16, 8
P_QKV = 0
P_REST = P_QKV + PAIRS_QKV
P_OUT0 = P_REST + PAIRS_REST
P_AB = P_OUT0 + PAIRS_OUT
P_Z = P_AB + PAIRS_AB
P_OUT1 = P_Z + PAIRS_Z
X_QKV = 8
X_K = X_QKV + 6
X_REST = X_K + 8
X_OUT0 = X_REST + 12
X_AB = X_OUT0 + 2
A_QKV, A_REST, A_OUT0, A_AB = 8, 14, 18, 20
TAPROWS = 72
EXPOS = HALO + DS


def trunk(nc, x_prompt, x_sample, cache_k, cache_v, state_conv, page_table, c_prompt, c_sample, ada_w, ada_b,
          norm_g, ab_w_in, a_ln_g, a_ln_b, a_ws, a_bs, ab_w_out, c_w_in, c_conv_w, c_conv_b, c_ln_g, c_ln_b,
          c_w_out, final_norm_g, y_prompt, y_sample, k_prompt, v_prompt, k_sample, v_sample, a_v_sample,
          conv_prompt, conv_sample):
    ada_v = ada_w.rearrange("l (k p) n -> l p k n", p=P)
    win_v = ab_w_in[0].rearrange("(k p) n -> p k n", p=P)
    wout_v = ab_w_out[0].rearrange("(k p) n -> p k n", p=P)
    cin_v = c_w_in[0].rearrange("(k p) n -> p k n", p=P)
    cout_v = c_w_out[0].rearrange("(k p) n -> p k n", p=P)
    kc_v = cache_k[0].rearrange("g r h d -> g r (h d)")
    vc_v = cache_v[0].rearrange("g r h d -> g r (h d)")
    xp_v = x_prompt[0]
    xs_v = x_sample.rearrange("s i d -> (s i) d")
    yp_v = y_prompt[0]
    ys_v = y_sample.rearrange("s i d -> (s i) d")
    kp_v = k_prompt[0, 0].rearrange("r h d -> r (h d)")
    vp_v = v_prompt[0, 0].rearrange("r h d -> r (h d)")
    ks_v = k_sample[0].rearrange("s i h d -> (s i) (h d)")
    vs_v = v_sample[0].rearrange("s i h d -> (s i) (h d)")
    av_v = a_v_sample[0].rearrange("s i d -> (s i) d")

    with ExitStack() as ctx:
        def sb(name, shape, dt=F32):
            return ctx.enter_context(nc.sbuf_tensor(name, shape, dt))

        def sem(name):
            return ctx.enter_context(nc.semaphore(name))

        XT = sb("XT", [P, KC, R])
        HH = sb("HH", [P, KC, R], F32R)
        HL = sb("HL", [P, KC, R], F32R)
        NACT = 56 * R
        ACTS = sb("ACTS", [P, NACT])
        WRAW = sb("WRAW", [P, 4, 4, 256])
        WHI = sb("WHI", [P, 4, 4, 256], F32R)
        WLO = sb("WLO", [P, 4, 4, 256], F32R)
        XR = sb("XR", [P, 4, 2048])
        CT = sb("CT", [P, KC, 32])
        ADA = sb("ADA", [P, 48, NC9])
        VT = sb("VT", [P, 208])
        IDENT = sb("IDENT", [P, P])
        ONES = sb("ONES", [P, P])
        SCR = sb("SCR", [P, 3 * R])
        CWT = sb("CWT", [P, KC, CW])
        PS = ctx.enter_context(nc.psum_tensor("PS", [P, 8, 512], F32))
        ACC = [0, 1, 2, 3]
        M0, M1, M2, M3 = 4, 5, 6, 7

        RB = SCR[:, 0:R]
        SQ = [SCR[:, R:2 * R], SCR[:, 2 * R:3 * R]]
        ADAS = SCR[:, R:R + 512]
        PTAB = SCR[0:1, R + 512:R + 576].bitcast(I32)
        RZ = SCR[:, 0:2]
        V_NORM = VT[:, 0:32]
        V_ALNG, V_ALNB = VT[:, 32:40], VT[:, 40:48]
        V_CB, V_CLNG, V_CLNB = VT[:, 48:64], VT[:, 64:80], VT[:, 80:96]
        V_FIN = VT[:, 96:112]
        V_ADAB = VT[:, 112:208]

        def A(lo, n, parts=P):
            return ACTS[0:parts, lo:lo + n]

        def chunks(first, n):
            return A(first * R, n * R).rearrange("p (c r) -> p c r", r=R)

        Q, K, V = chunks(0, 8), chunks(8, 8), chunks(16, 8)
        ZB, U, VA, ZA = chunks(24, 8), chunks(32, 8), chunks(40, 8), chunks(48, 8)
        XROW = [A(0, D), A(2048, D), A(4096, D, 32)]
        CROW = A(6144, D, 32)
        VROWS1, VROWS2 = A(8192, P, 112), A(8320, P, 96)
        CWROW = A(8448, D, CW)
        HOFF = KC * (SEQ + HALO + NS * EXPOS)
        HF = A(HOFF, KC * R).rearrange("p (c r) -> p c r", r=R)
        o = 24 * R
        KROW = [A(o, DA), A(o + 1024, DA), A(o + 2048, DA, 32)]
        VROW = [A(o + 3072, DA), A(o + 4096, DA)]
        PMASK = A(o + 5120, 384)
        PP = [A(o + 5504, 384), A(o + 5888, 384)]
        PPT = [A(o + 6272, 384), A(o + 6656, 384)]
        PST = A(o + 7040, 16)
        KT = [A(o, 4096).rearrange("p (b j h n) -> p b j h n", b=2, j=4, h=2),
              WRAW[:].rearrange("p c k n -> p (c k n)").rearrange("p (b j h n) -> p b j h n", b=2, j=4, h=2)]
        QM = A(o + 4096, 2048).rearrange("p (s h c) -> p s h c", s=NS, h=HEADS)
        SROW = A(o + 6144, 1152)
        BIAS = A(o + 7296, 1024)
        KSM = A(o + 8320, 512)
        OWN = KSM[:, 0:64].rearrange("p (b n) -> p b n", b=2)
        GATE = KSM[:, 64:68]
        CMP = KSM[:, 68:84].rearrange("p (n m) -> p n m", n=4)
        PEN = KSM[:, 84:88]
        NMAX = KSM[:, 88:89]
        ZSUM = KSM[:, 89:90]
        QROW, SLROW = KSM[:, 90:91], KSM[:, 91:92]
        IOTA4 = KSM[:, 96:128]
        OMASK = KSM[:, 128:192].rearrange("p (b n) -> p b n", b=2)
        OTMP = KSM[:, 192:256].rearrange("p (b n) -> p b n", b=2)
        ROWSEED = KSM[:, 256:384]
        PT = A(8 * R, 2304).rearrange("p (b t c) -> p b t c", b=2, t=9)
        VNEW = A(16 * R, DA)
        OROW = A(16 * R + 1024, DA)
        PTS = A(16 * R + 2048, 256).rearrange("p (t c) -> p t c", t=2)
        WST = A(8 * R, 1024).rearrange("p (g t) -> p g t", g=GC)
        WSROW = A(8 * R + 1024, 1024).rearrange("p (g t) -> p g t", g=GC)
        W4 = A(8 * R + 2048, 128)
        VAROW = A(16 * R, 2048).rearrange("p (c n) -> p c n", c=2)
        BSB = A(24 * R, 1024).rearrange("p (g t) -> p g t", g=GC)
        AVROW = A(24 * R + 1024, DA, 32)
        GP = SEQ + HALO + NS * EXPOS
        GLU = A(0, KC * GP).rearrange("p (c n) -> p c n", n=GP)
        Y = HF
        STROW = [A(HOFF, D, 120), A(HOFF + D, D, 120)]
        EX = A(HOFF + KC * R, EXPOS * TAPROWS).rearrange("p (o l) -> p o l", l=TAPROWS)
        Z = XR[:].rearrange("p a n -> p (a n)")[:, 0:KC * R].rearrange("p (c r) -> p c r", r=R)
        YROW = [A(HOFF, D), A(HOFF + D, D), A(HOFF + 2 * D, D, 32)]

        s_rows = sem("rows_loaded")
        s_cz = sem("crow_zeroed")
        s_vec = sem("vectors_loaded")
        s_ptab = sem("page_table_loaded")
        s_ident = sem("identity_built")
        s_setup_pe = sem("setup_transposed")
        s_setup_cp = sem("setup_copied")
        s_silu, s_crow = sem("cond_silu"), sem("cond_loaded")
        s_pmx, s_kv, s_res, s_res2, ada_part = (sem("pa_max"), sem("kv_stored"), sem("residual_added"),
                                                sem("gated_samples"), sem("ada_reduced"))
        g_wld, g_w4, g_yb, g_av, g_avst, g_ln, g_ya, g_mean, g_vn, g_vca, g_vcd, g_mr = (sem(n) for n in (
            "ws_landed", "w4_landed", "yb_ready", "av_rows", "av_stored", "va_centred", "ya_ready", "va_mean",
            "va_normalised", "varow_by_act", "varow_by_dve", "mix_added"))
        cl_rdy, ln_mean, ln_y, ln_r, ln_s, ln_z, f_cpa, f_cpd, s_fin = (sem(n) for n in (
            "conv_tail_saved", "cln_mean", "cln_centred", "cln_scaled", "cln_silu", "cln_gated", "final_by_act",
            "final_by_dve", "y_stored"))
        w_raw = [sem(f"w_raw{c}") for c in range(4)]
        w_hi, w_lo, w_used = sem("w_hi"), sem("w_lo"), sem("w_used")
        acc_free = sem("acc_free")
        x_rdy = [sem(f"x_rdy{c}") for c in range(4)]
        x_used = sem("x_used")
        ada_cp, ada_tr, ada_done = sem("ada_copied"), sem("ada_turned"), sem("ada_done")
        s_sq, s_sqmm = sem("squares_ready"), sem("squares_summed")
        s_hf, s_hh, s_hl = sem("rows_normalised"), sem("input_hi"), sem("input_lo")
        s_act, s_dve, s_pool = sem("act_chain"), sem("dve_chain"), sem("pool_chain")
        s_stat, s_root = sem("statistic_ready"), sem("root_ready")
        s_rowt, s_rowc, s_rowc2 = sem("kv_rows_turned"), sem("kv_rows_copied"), sem("kv_rows_out")
        s_qs = sem("q_scaled")
        s_pm = sem("prompt_mask")
        s_ps, s_pe1, s_pn, s_pt, s_pc, s_po, s_pf = (sem("pa_scores"), sem("pa_exp"), sem("pa_norm"), sem("pa_turned"),
                                                     sem("pa_copied"), sem("pa_product"), sem("pa_out"))
        s_pb = sem("pa_biased")
        s_qm, s_consts = sem("q_masked"), sem("k_constants")
        s_own, s_ownc = sem("own_scores"), sem("own_saved")
        kt_tr, kt_a, kt_d, ks_free = sem("kt_turned"), sem("kt_by_act"), sem("kt_by_dve"), sem("k_scores_read")
        ks_head = sem("k_head_pair_done")
        s_max, s_exp, s_ptt, s_ptc = sem("sm_max"), sem("sm_exp"), sem("probs_turned"), sem("probs_saved")
        s_vz = sem("vnew_ready")
        pts_rdy = sem("probs_staged")
        o_row, o_tr, o_cp = sem("o_row"), sem("o_turned"), sem("o_copied")
        g_ws, g_wst, g_wsc, g_act, g_vt, g_mix, g_bs = (sem("ws_masked"), sem("ws_turned"), sem("ws_copied"),
            sem("gate_acts"), sem("va_turned"), sem("mixed"), sem("bs_loaded"))
        st_ld, st_tr, st_cp = sem("state_loaded"), sem("state_turned"), sem("state_copied")
        s_glu, s_ex, s_tap = sem("glu_ready"), sem("taps_spread"), sem("taps_done")
        cp_tr, cp_cp = sem("conv_rows_turned"), sem("conv_rows_copied")
        f_tr, f_row = sem("final_turned"), sem("final_scaled")
        s_out = sem("outputs_stored")
        s_zero = sem("halo_zeroed")

        block = ctx.enter_context(nc.Block())
        OUTS = [0]
        chain_n = {"act": 0, "dve": 0, "pool": 0}
        chain_sem = {"act": s_act, "dve": s_dve, "pool": s_pool}

        def link(eng, who, ins):
            chain_n[who] += 1
            ins.then_inc(chain_sem[who], 1)
            eng.wait_ge(chain_sem[who], chain_n[who])

        def bc(ap, shape):
            return ap.to_broadcast(shape)

        def part(ap):
            return ap.rearrange("p c (s i) -> p c s i", i=DS)

        def store(eng, dst, src):
            eng.dma_start(dst, src).then_inc(s_out, 16)
            OUTS[0] += 1

        def load_w(sp, p, c, w_v, col, first=False, turn=0):
            k = 4 * ((c + turn) % 4)
            if not first:
                sp.wait_ge(w_lo, 4 * (p - 1) + c + 1)
            sp.dma_start(WRAW[:, c], w_v[:, k:k + 4, bass.ds(col, 256)]).then_inc(w_raw[c], 16)

        def load_pair(sp, p, w_v, col, first=False, turn=0):
            for c in range(4):
                load_w(sp, p, c, w_v, col, first, turn)

        def split_hi(act, p, c, first=False):
            act.wait_ge(w_raw[c], 16 * p + 16)
            if not first:
                act.wait_ge(w_used, 4 * (p - 1) + c + 1)
            act.activation(WHI[:, c], WRAW[:, c], ACT.Copy).then_inc(w_hi, 1)

        def split_lo(eng, p, c):
            eng.wait_ge(w_hi, 4 * p + c + 1)
            eng.tensor_tensor(WLO[:, c], WRAW[:, c], WHI[:, c].bitcast(F32), ALU.subtract).then_inc(w_lo, 1)

        def split_hi4(act, p, first=False):
            for c in range(4):
                split_hi(act, p, c, first)

        def split_lo4(eng, p):
            for c in range(4):
                split_lo(eng, p, c)

        def products(pe, p, parity, inputs, first=False, turn=0):
            if not first:
                pe.wait_ge(acc_free, p - 1)
            for c in range(4):
                pe.wait_ge(w_lo, 4 * p + c + 1)
                pe.wait_ge(s_hl, inputs + 4 * c + 4)
                for kk in range(4):
                    k = 4 * ((c + turn) % 4) + kk
                    for n in range(2):
                        out = PS[:, ACC[2 * parity + n], 0:R]
                        whi, wlo = WHI[:, c, kk, n * P:(n + 1) * P], WLO[:, c, kk, n * P:(n + 1) * P]
                        s, e = c == 0 and kk == 0, c == 3 and kk == 3
                        pe.matmul(out, whi, HH[:, k, :], start=s, stop=False)
                        pe.matmul(out, whi, HL[:, k, :], start=False, stop=False)
                        last = pe.matmul(out, wlo, HH[:, k, :], start=False, stop=e)
                last.then_inc(w_used, 1)

        def copy_out(dve, p, parity, n):
            dve.wait_ge(w_used, 4 * p + 4)
            dst = A(n * R, 2 * R) if isinstance(n, int) else ACTS[:, bass.ds(n * R, 2 * R)]
            dve.tensor_copy(dst.rearrange("p (c r) -> p c r", r=R),
                            PS[:, 2 * parity:2 * parity + 2, 0:R]).then_inc(acc_free, 1)

        def add_gated(dve, p, parity, n, seq):
            dve.wait_ge(w_used, 4 * p + 4)
            if seq is not None:
                dve.wait_ge(s_res, seq)
            gate = ADA[:, bass.ds(32 + n, 2), :]
            tmp = RB[:, 0:64].rearrange("p (c s i) -> p c s i", c=2, i=DS)
            acc = PS[:, 2 * parity:2 * parity + 2, SR0:R]
            dve.tensor_tensor(tmp, part(acc), bc(gate[:, :, 1:NC9].unsqueeze(3), [P, 2, NS, DS]),
                              ALU.mult).then_inc(s_res2, 1)
            for x in range(2):
                xt = XT[:, bass.ds(n + x, 1), 0:SEQ].rearrange("p c r -> p (c r)")
                g0 = ADA[:, bass.ds(32 + n + x, 1), 0:1].rearrange("p a b -> p (a b)")
                last = dve.scalar_tensor_tensor(xt, PS[:, 2 * parity + x, 0:SEQ], g0, xt, ALU.mult, ALU.add)
            last.then_inc(acc_free, 1)
            dve.wait_ge(s_res2, (0 if seq is None else seq) + 1)
            xs = XT[:, bass.ds(n, 2), SR0:R]
            dve.tensor_tensor(xs, xs, tmp.rearrange("p c s i -> p c (s i)"), ALU.add).then_inc(s_res, 1)

        def load_ada(sp, quad, layer, col, first=False):
            for c in range(4):
                if not first:
                    sp.wait_ge(x_used, 4 * (quad - 1) + c + 1)
                for half in range(2):
                    k = 4 * c + 2 * half
                    sp.dma_start(XR[:, c, half * 1024:(half + 1) * 1024].rearrange("p (k n) -> p k n", k=2),
                                 ada_v[layer, :, k:k + 2, bass.ds(col, 512)]).then_inc(x_rdy[c], 16)

        def ada_sum_block(pe, quad, a, first=False):
            if not first:
                pe.wait_ge(ada_cp, a)
            for c in range(4):
                pe.wait_ge(x_rdy[c], 32 * quad + 32)
                for kk in range(4):
                    last = pe.matmul(PS[32 * kk:32 * kk + 32, M0, :], CT[:, 4 * c + kk, :],
                                     XR[:, c, kk * 512:(kk + 1) * 512], start=c == 0, stop=c == 3)
                last.then_inc(x_used, 1)

        def ada_copy(act, quad, a, first=False):
            act.wait_ge(x_used, 4 * quad + 4)
            if not first:
                act.wait_ge(ada_tr, a)
            act.activation(ADAS, PS[:, M0, :], ACT.Copy).then_inc(ada_cp, 1)

        def ada_turn(pe, a, first=False):
            pe.wait_ge(ada_cp, a + 1)
            if not first:
                pe.wait_ge(ada_done, a)
            for m in range(4):
                last = pe.transpose(PS[:, M1, m * P:(m + 1) * P], ADAS[:, m * P:(m + 1) * P], IDENT[:])
            last.then_inc(ada_tr, 1)

        def ada_reduce(dve, a, b, layer):
            dve.wait_ge(ada_tr, a + 1)
            dst = ADA[:, bass.ds(4 * b, 4), :]
            src = PS[:, M1, :].rearrange("p (m j r) -> p m r j", m=4, j=4)[:, :, 0:NC9, :]
            dve.tensor_reduce(dst, src, AX.X, ALU.add).then_inc(ada_part, 1)
            dve.wait_ge(ada_part, a + 1)
            bias = V_ADAB[:, bass.ds(48 * layer + 4 * b, 4)]
            dve.tensor_tensor(dst, dst, bc(bias.unsqueeze(2), [P, 4, NC9]), ALU.add).then_inc(ada_done, 1)

        def scale_times_gain(dve, layer):
            sc = ADA[:, 16:32, :]
            link(dve, "dve", dve.tensor_scalar(sc, sc, 1.0, None, ALU.add))
            link(dve, "dve", dve.tensor_tensor(sc, sc, bc(V_NORM[:, 16 * layer:16 * layer + 16].unsqueeze(2), [P, 16, NC9]), ALU.mult))

        def squares(act, src, n, base):
            for k in range(n):
                if base + k >= 2:
                    act.wait_ge(s_sqmm, base + k - 1)
                act.activation(SQ[k % 2], src[:, k, :], ACT.Square).then_inc(s_sq, 1)

        def sum_squares(pe, n, base, bank):
            for k in range(n):
                pe.wait_ge(s_sq, base + k + 1)
                pe.matmul(PS[:, bank, 0:R], ONES[:], SQ[k % 2], start=k == 0, stop=k == n - 1).then_inc(s_sqmm, 1)

        def variance_inverse(dve, base, bank, width, stat):
            dve.wait_ge(s_sqmm, base)
            link(dve, "dve", dve.tensor_scalar(RB, PS[:, bank, 0:R], 1.0 / width, EPS, ALU.mult, ALU.add))
            dve.reciprocal(RB, RB).then_inc(s_stat, 1)

        def root(act, n):
            act.wait_ge(s_stat, n)
            act.activation(RB, RB, ACT.Sqrt).then_inc(s_root, 1)

        def normalise(dve, n, base):
            dve.wait_ge(s_root, n)
            xs, hs = part(XT[:, :, SR0:R]), part(HF[:, :, SR0:R])
            link(dve, "dve", dve.tensor_tensor(HF[:, :, SR0:R], XT[:, :, SR0:R],
                                               bc(RB[:, SR0:R].unsqueeze(1), [P, KC, NS * DS]), ALU.mult))
            link(dve, "dve", dve.tensor_tensor(hs, hs, bc(ADA[:, 16:32, 1:NC9].unsqueeze(3), [P, KC, NS, DS]), ALU.mult))
            link(dve, "dve", dve.tensor_tensor(hs, hs, bc(ADA[:, 0:16, 1:NC9].unsqueeze(3), [P, KC, NS, DS]), ALU.add))
            for k in range(KC + 2):
                if k < KC:
                    dve.tensor_tensor(HF[:, k, 0:SEQ], XT[:, k, 0:SEQ], RB[:, 0:SEQ], ALU.mult).then_inc(s_hf, 1)
                if k >= 2:
                    lo_part(dve, HF, k - 2, k - 2, base + k - 2)

        def lo_part(dve, src, k, dst, count):
            dve.wait_ge(s_hh, count + 1)
            dve.tensor_tensor(HL[:, dst, :], src[:, k, :], HH[:, dst, :].bitcast(F32), ALU.subtract).then_inc(s_hl, 1)

        def modulate(act, hf_base, used):
            if used:
                act.wait_ge(w_used, used)
            for k in range(KC):
                act.wait_ge(s_hf, hf_base + k + 1)
                link(act, "act", act.activation(HF[:, k, 0:SEQ], HF[:, k, 0:SEQ], ACT.Identity,
                                                bias=ADA[:, k, 0:1], scale=ADA[:, 16 + k, 0:1]))
                act.activation(HH[:, k, :], HF[:, k, :], ACT.Copy).then_inc(s_hh, 1)

        def start_act(act):
            act.wait_ge(s_cz, 1)
            act.dma_start(CROW[0:1, :], c_prompt).then_inc(s_crow, 16)
            act.dma_start(CROW[1:NC9, :], c_sample).then_inc(s_crow, 16)
            act.dma_start(XROW[0], xp_v[0:P]).then_inc(s_rows, 16)
            act.dma_start(XROW[1], xp_v[P:2 * P]).then_inc(s_rows, 16)
            act.dma_start(XROW[2], xs_v).then_inc(s_rows, 16)
            at = 0
            for t, rows in ((norm_g.rearrange("l (k p) -> (l k) p", p=P), 32),
                            (a_ln_g.rearrange("l (k p) -> (l k) p", p=P), 8),
                            (a_ln_b.rearrange("l (k p) -> (l k) p", p=P), 8),
                            (c_conv_b.rearrange("l (k p) -> (l k) p", p=P), 16),
                            (c_ln_g.rearrange("l (k p) -> (l k) p", p=P), 16),
                            (c_ln_b.rearrange("l (k p) -> (l k) p", p=P), 16),
                            (final_norm_g.rearrange("(k p) -> k p", p=P), 16)):
                act.dma_start(VROWS1[at:at + rows, :], t).then_inc(s_vec, 16)
                at += rows
            act.dma_start(VROWS2, ada_b.rearrange("l (k p) -> (l k) p", p=P)).then_inc(s_vec, 16)
            act.dma_start(CWROW, c_conv_w[0]).then_inc(s_vec, 16)
            act.wait_ge(s_crow, 32)
            act.activation(CROW, CROW, ACT.Silu).then_inc(s_silu, 1)
            ada_copy(act, 0, 0, first=True)
            with act.Fori(1, 4) as a:
                ada_copy(act, a, a)
            with act.Fori(4, 6) as a:
                ada_copy(act, a, a)
            act.wait_ge(ada_tr, 6)
            act.wait_ge(s_setup_cp, 4 + KC)
            squares(act, XT, KC, 0)
            act.wait_ge(s_sqmm, KC)
            act.dma_start(PTAB, page_table.rearrange("(a s) t -> a (s t)", a=1)).then_inc(s_ptab, 16)
            with act.Fori(6, 8) as a:
                ada_copy(act, a, a)
            root(act, 1)
            split_hi4(act, 0, first=True)
            modulate(act, 0, 0)

        def start_pe(pe):
            pe.wait_ge(s_ident, 2)
            pe.wait_ge(s_silu, 1)
            for k in range(KC):
                last = pe.transpose(PS[:, M3, k * 32:(k + 1) * 32], CROW[:, k * P:(k + 1) * P], IDENT[0:32, 0:32])
            last.then_inc(s_setup_pe, 1)
            pe.wait_ge(s_vec, 9 * 16)
            pe.transpose(PS[:, M2, 0:112], VROWS1, IDENT[0:112, 0:112])
            pe.transpose(PS[:, M2, 112:208], VROWS2, IDENT[0:96, 0:96]).then_inc(s_setup_pe, 1)
            pe.wait_ge(s_setup_cp, 1)
            for k in range(KC):
                last = pe.transpose(PS[:, M3, k * CW:(k + 1) * CW], CWROW[:, k * P:(k + 1) * P], IDENT[0:CW, 0:CW])
            last.then_inc(s_setup_pe, 1)
            pe.wait_ge(s_consts, 1)
            pe.transpose(PS[:, ACC[3], 0:P], ROWSEED, IDENT[:]).then_inc(s_setup_pe, 1)
            ada_sum_block(pe, 0, 0, first=True)
            ada_sum_block(pe, 1, 1)
            ada_turn(pe, 0, first=True)
            with pe.Fori(2, 4) as a:
                ada_sum_block(pe, a, a)
                ada_turn(pe, a - 1)
            ada_turn(pe, 3)
            pe.wait_ge(s_rows, 48)
            for k in range(KC):
                if k % 4 == 3 or k >= 4:
                    pe.wait_ge(s_setup_cp, 4 + max(0, k - 3))
                for t, rows in ((0, P), (1, P), (2, NS * DS)):
                    last = pe.transpose(PS[:, ACC[k % 4], t * P:t * P + rows], XROW[t][:, k * P:(k + 1) * P],
                                        IDENT[0:rows, 0:rows])
                last.then_inc(s_setup_pe, 1)
            with pe.Fori(4, 6) as a:
                ada_sum_block(pe, a, a)
                ada_turn(pe, a)
            sum_squares(pe, KC, 0, M3)
            with pe.Fori(6, 8) as a:
                ada_sum_block(pe, a, a)
                ada_turn(pe, a)

        def start_dve(dve):
            dve.wait_ge(s_setup_pe, 1)
            dve.tensor_copy(CT[:], PS[:, M3, :].rearrange("p (k c) -> p k c", c=32)).then_inc(s_setup_cp, 1)
            dve.wait_ge(s_setup_pe, 2)
            dve.tensor_copy(VT[:], PS[:, M2, 0:208]).then_inc(s_setup_cp, 1)
            dve.wait_ge(s_setup_pe, 3)
            dve.tensor_copy(CWT[:], PS[:, M3, 0:KC * CW].rearrange("p (k c) -> p k c", c=CW)).then_inc(s_setup_cp, 1)
            dve.wait_ge(s_setup_pe, 4)
            dve.tensor_copy(QROW, PS[:, ACC[3], 0:1])
            link(dve, "dve", dve.tensor_copy(SLROW, PS[:, ACC[3], 32:33]))
            dve.wait_ge(s_consts, 2)
            dve.tensor_scalar(BIAS, BIAS, SLROW, None, ALU.mult)
            for b in range(2):
                link(dve, "dve", dve.tensor_scalar(OTMP[:, b, :], IOTA4, QROW, None, ALU.is_le))
            link(dve, "dve", dve.tensor_tensor(OTMP, OTMP, OMASK, ALU.mult))
            link(dve, "dve", dve.tensor_scalar(OTMP, OTMP, -NEG, NEG, ALU.mult, ALU.add))
            for b in range(2):
                last = dve.scalar_tensor_tensor(OMASK[:, b, :], IOTA4, SLROW, OTMP[:, b, :], ALU.mult, ALU.add)
            last.then_inc(s_setup_cp, 1)
            with dve.Fori(0, 4) as a:
                ada_reduce(dve, a, a, 0)
            for k in range(KC):
                dve.wait_ge(s_setup_pe, 5 + k)
                dve.tensor_copy(XT[:, k, :], PS[:, ACC[k % 4], 0:R]).then_inc(s_setup_cp, 1)
            with dve.Fori(4, 6) as a:
                ada_reduce(dve, a, a, 0)
            variance_inverse(dve, KC, M3, D, 1)
            with dve.Fori(6, 8) as a:
                ada_reduce(dve, a, a, 0)
            dve.wait_ge(ada_done, 8)
            scale_times_gain(dve, 0)
            split_lo4(dve, 0)
            normalise(dve, 1, 0)

        def start_pool(pool):
            pool.memset(CROW, 0.0).then_inc(s_cz, 1)
            link(pool, "pool", pool.memset(IDENT[:], 0.0))
            pool.affine_select(out=IDENT[:], in_=IDENT[:], compare_op=ALU.not_equal, fill=1.0, base=0,
                               pattern=[[-1, P]], channel_multiplier=1).then_inc(s_ident, 1)
            pool.memset(ONES[:], 1.0).then_inc(s_ident, 1)
            link(pool, "pool", pool.memset(ROWSEED, 0.0))
            seed = ROWSEED.rearrange("p (j h q) -> p j h q", j=4, h=HEADS)
            pool.iota(ROWSEED[0:1, :], [[0, 4], [0, HEADS], [1, DS]], base=0, channel_multiplier=0,
                      allow_small_or_imprecise_dtypes=True)
            for h in range(HEADS):
                last = pool.memset(seed[32:33, :, h, :], SLOPES[h])
            link(pool, "pool", last)
            pool.sem_inc(s_consts, 1)
            pool.iota(BIAS, [[1, PAST]], base=-PAST, channel_multiplier=0, allow_small_or_imprecise_dtypes=True)
            pool.iota(IOTA4, [[0, NS], [1, DS]], base=0, channel_multiplier=0, allow_small_or_imprecise_dtypes=True)
            link(pool, "pool", pool.memset(OMASK, 0.0))
            for b in range(2):
                for j in range(4):
                    s = 4 * b + j
                    last = pool.memset(OMASK[32 * j:32 * j + 32, b, DS * s:DS * s + DS], 1.0)
            link(pool, "pool", last)
            pool.sem_inc(s_consts, 1)
            pool.wait_ge(s_hl, KC)
            pool.iota(PMASK[:, 0:P], [[1, P]], base=0, channel_multiplier=-1, allow_small_or_imprecise_dtypes=True)
            link(pool, "pool", pool.iota(PMASK[:, P:384], [[1, 2 * P]], base=-P, channel_multiplier=-1,
                                         allow_small_or_imprecise_dtypes=True))
            pool.affine_select(out=PMASK[:, 0:P], in_=PMASK[:, 0:P], compare_op=ALU.is_ge, fill=-1e33, base=0,
                               pattern=[[-1, P]], channel_multiplier=1)
            pool.affine_select(out=PMASK[:, P:384], in_=PMASK[:, P:384], compare_op=ALU.is_ge, fill=-1e33, base=P,
                               pattern=[[-1, 2 * P]], channel_multiplier=1).then_inc(s_pm, 1)

        def qkv_pe(pe):
            ada_sum_block(pe, X_QKV, A_QKV)
            products(pe, 0, 0, 0, first=True)
            products(pe, 1, 1, 0, first=True)
            ada_turn(pe, A_QKV)
            with pe.Fori(1, 6) as i:
                ada_sum_block(pe, X_QKV + i, A_QKV + i)
                products(pe, 2 * i, 0, 0)
                products(pe, 2 * i + 1, 1, 0)
                ada_turn(pe, A_QKV + i)

        def qkv_act(act):
            ada_copy(act, X_QKV, A_QKV)
            split_hi4(act, 1)
            with act.Fori(1, 6) as i:
                split_hi4(act, 2 * i)
                ada_copy(act, X_QKV + i, A_QKV + i)
                split_hi4(act, 2 * i + 1)

        def qkv_dve(dve):
            split_lo4(dve, 1)
            copy_out(dve, 0, 0, 0)
            with dve.Fori(1, 6) as i:
                split_lo4(dve, 2 * i)
                copy_out(dve, 2 * i - 1, 1, 4 * i - 2)
                ada_reduce(dve, A_QKV - 1 + i, i - 1, 1)
                split_lo4(dve, 2 * i + 1)
                copy_out(dve, 2 * i, 0, 4 * i)
            copy_out(dve, 11, 1, 22)
            ada_reduce(dve, A_QKV + 5, 5, 1)
            dve.wait_ge(acc_free, 12)
            dve.tensor_scalar(Q, Q, QSCALE, None, ALU.mult).then_inc(s_qs, 1)

        ROW_FILLS = ([(K, rt, half) for rt in range(3) for half in range(2)]
                     + [(V, rt, half) for rt in range(2) for half in range(2)])

        def rows_pe(pe):
            pe.wait_ge(acc_free, 12)
            for f, (t, rt, half) in enumerate(ROW_FILLS):
                if f >= 4:
                    pe.wait_ge((s_rowc, s_rowc2)[f % 2], (f - 4) // 2 + 1)
                rows = P if rt < 2 else NS * DS
                for x in range(4):
                    last = pe.transpose(PS[0:rows, ACC[f % 4], x * P:(x + 1) * P],
                                        t[:, 4 * half + x, rt * P:rt * P + rows], IDENT[:])
                last.then_inc(s_rowt, 1)
            for half in range(2):
                for x in range(4):
                    last = pe.transpose(PS[0:NS * DS, M2 + half, x * P:(x + 1) * P], V[:, 4 * half + x, SR0:R], IDENT[:])
            last.then_inc(s_rowt, 1)

        def row_copy(eng, f):
            t, rt, half = ROW_FILLS[f]
            rows = P if rt < 2 else NS * DS
            dst = (KROW if f < 6 else VROW)[rt][:, half * 512:(half + 1) * 512]
            eng.wait_ge(s_rowt, f + 1)
            if eng is nc.scalar:
                return nc.scalar.activation(dst, PS[0:rows, ACC[f % 4], :], ACT.Copy)
            return nc.vector.tensor_copy(dst, PS[0:rows, ACC[f % 4], :])

        def rows_act(act):
            for f in range(0, 10, 2):
                row_copy(nc.scalar, f).then_inc(s_rowc, 1)

        def rows_dve(dve):
            for f in range(1, 10, 2):
                row_copy(nc.vector, f).then_inc(s_rowc2, 1)
            dve.wait_ge(s_rowt, 11)
            link(dve, "dve", dve.memset(VNEW, 0.0))
            dve.tensor_copy(VNEW[0:NS * DS, :].rearrange("p (a n) -> p a n", a=2), PS[0:NS * DS, M2:M3 + 1, :]).then_inc(s_vz, 1)

        def rows_pool(pool):
            for sem_c, sem_d, dst, src in ((2, 1, kp_v[0:P], KROW[0]), (2, 2, kp_v[P:2 * P], KROW[1]),
                                           (3, 3, ks_v, KROW[2]), (4, 4, vp_v[0:P], VROW[0]), (5, 5, vp_v[P:2 * P], VROW[1])):
                pool.wait_ge(s_rowc, sem_c)
                pool.wait_ge(s_rowc2, sem_d)
                pool.dma_start(dst, src).then_inc(s_kv, 16)
            pool.wait_ge(s_vz, 1)
            pool.dma_start(vs_v, VNEW[0:NS * DS, :]).then_inc(s_kv, 16)

        def prompt_pe(pe):
            pe.wait_ge(s_qs, 1)
            pe.wait_ge(s_rowc, 5)
            pe.wait_ge(s_rowc2, 5)
            pe.wait_ge(s_vz, 1)
            for h in range(HEADS + 2):
                if h < HEADS:
                    if h >= 2:
                        pe.wait_ge(s_pb, h - 1)
                    bank = ACC[h % 2]
                    pe.matmul(PS[:, bank, 0:P], Q[:, h, 0:P], K[:, h, 0:P], start=True, stop=True)
                    pe.matmul(PS[:, bank, P:384], Q[:, h, P:2 * P], K[:, h, 0:2 * P], start=True, stop=True).then_inc(s_ps, 1)
                g = h - 1
                if 0 <= g < HEADS:
                    pe.wait_ge(s_pn, g + 1)
                    if g >= 2:
                        pe.wait_ge(s_pc, g - 1)
                    for t in range(3):
                        last = pe.transpose(PS[:, ACC[2 + g % 2], t * P:(t + 1) * P], PP[g % 2][:, t * P:(t + 1) * P], IDENT[:])
                    last.then_inc(s_pt, 1)
                g = h - 2
                if 0 <= g < HEADS:
                    pe.wait_ge(s_pc, g + 1)
                    if g >= 2:
                        pe.wait_ge(s_pf, g - 1)
                    bank, pt = (M2, M3)[g % 2], PPT[g % 2]
                    v0, v1 = (VROW[t][:, g * P:(g + 1) * P] for t in range(2))
                    pe.matmul(PS[:, bank, 0:P], v0, pt[:, 0:P], start=True, stop=True)
                    pe.matmul(PS[:, bank, P:2 * P], v0, pt[:, P:2 * P], start=True, stop=False)
                    pe.matmul(PS[:, bank, P:2 * P], v1, pt[:, 2 * P:384], start=False, stop=True).then_inc(s_po, 1)

        def pstat(h):
            return PST[:, 6 * (h % 2):6 * (h % 2) + 6]

        def prompt_act(act):
            for h in range(HEADS + 1):
                if h < HEADS:
                    act.wait_ge(s_pmx, h + 1)
                    pp, st = PP[h % 2], pstat(h)
                    act.activation(pp[:, 0:P], pp[:, 0:P], ACT.Exp, bias=st[:, 0:1], accum_out=st[:, 2:3])
                    act.activation(pp[:, P:384], pp[:, P:384], ACT.Exp, bias=st[:, 1:2], accum_out=st[:, 3:4]).then_inc(s_pe1, 1)
                g = h - 1
                if g >= 0:
                    act.wait_ge(s_pt, g + 1)
                    if g >= 2:
                        act.wait_ge(s_po, g - 1)
                    act.activation(PPT[g % 2], PS[:, ACC[2 + g % 2], 0:384], ACT.Copy).then_inc(s_pc, 1)

        def prompt_dve(dve):
            dve.wait_ge(s_pm, 1)
            for h in range(HEADS + 2):
                if h < HEADS:
                    dve.wait_ge(s_ps, h + 1)
                    if h >= 2:
                        dve.wait_ge(s_pt, h - 1)
                    pp, st = PP[h % 2], pstat(h)
                    dve.scalar_tensor_tensor(pp, PMASK, SLOPES[h], PS[:, ACC[h % 2], 0:384], ALU.mult, ALU.add).then_inc(s_pb, 1)
                    dve.wait_ge(s_pb, h + 1)
                    dve.tensor_reduce(st[:, 0:1], pp[:, 0:P], AX.X, ALU.max, negate=True)
                    dve.tensor_reduce(st[:, 1:2], pp[:, P:384], AX.X, ALU.max, negate=True).then_inc(s_pmx, 1)
                g = h - 1
                if 0 <= g < HEADS:
                    pp, st = PP[g % 2], pstat(g)
                    dve.wait_ge(s_pe1, g + 1)
                    link(dve, "dve", dve.reciprocal(st[:, 4:6], st[:, 2:4]))
                    dve.tensor_scalar(pp[:, 0:P], pp[:, 0:P], st[:, 4:5], None, ALU.mult)
                    dve.tensor_scalar(pp[:, P:384], pp[:, P:384], st[:, 5:6], None, ALU.mult).then_inc(s_pn, 1)
                g = h - 2
                if 0 <= g < HEADS:
                    dve.wait_ge(s_po, g + 1)
                    dve.tensor_copy(Q[:, g, 0:SEQ], PS[:, (M2, M3)[g % 2], 0:SEQ]).then_inc(s_pf, 1)

        def load_pages(sp, quad, b, tp, cache):
            for j in range(4):
                sp.wait_ge(x_used, 4 * (quad - 1) + j + 1)
                for t in range(2):
                    page = sp.value_load(PTAB[0:1, bass.ds((4 * b + j) * NPAGE + 2 * tp + t, 1)],
                                         min_val=0, max_val=cache.shape[0] - 1)
                    sp.dma_start(XR[:, j, t * 1024:(t + 1) * 1024], cache[bass.ds(page, 1)]).then_inc(x_rdy[j], 16)

        def kphase_pe(pe):
            pe.wait_ge(s_qm, 1)
            for b in range(2):
                for h in range(HEADS):
                    for j in range(4):
                        last = pe.matmul(PS[32 * j:32 * j + 32, M1, 32 * b:32 * b + 32], QM[:, 4 * b + j, h, :],
                                         K[:, h, SR0:R], start=h == 0, stop=h == HEADS - 1)
            last.then_inc(s_own, 1)
            for _ in range(4):
                pe.sem_inc(ks_head, 1)
            for b in range(2):
                with pe.Fori(0, 4) as tp:
                    q = 4 * b + tp
                    for j in range(4):
                        pe.wait_ge(x_rdy[j], 32 * (X_K + 1) + 32 * q)
                        for hh in range(4):
                            pe.wait_ge((kt_a, kt_d)[hh % 2], 8 * q + 2 * j + hh // 2 + 1)
                            for h2 in range(2):
                                for t in range(2):
                                    h = 2 * hh + h2
                                    last = pe.transpose(PS[:, ACC[hh], (2 * h2 + t) * P:(2 * h2 + t + 1) * P],
                                                        XR[:, j, t * 1024 + h * P:t * 1024 + (h + 1) * P], IDENT[:])
                                    if j and h == 0 and t == 0:
                                        last.then_inc(x_used, 1)
                            last.then_inc(kt_tr, 1)
                    pe.wait_ge(ks_free, q + 1)
                    for hh in range(4):
                        pe.wait_ge((kt_a, kt_d)[hh % 2], 8 * q + 9 + hh // 2)
                        for h2 in range(2):
                            h = 2 * hh + h2
                            for j in range(4):
                                last = pe.matmul(PS[32 * j:32 * j + 32, M0, 0:BLOCK], QM[:, 4 * b + j, h, :],
                                                 KT[hh // 2][:, hh % 2, j, h2, :], start=h == 0, stop=h == HEADS - 1)
                                if h == 0 and j == 0:
                                    last.then_inc(x_used, 1)
                        last.then_inc(ks_head, 1)
                pe.wait_ge(s_exp, b + 1)
                pe.wait_ge(kt_a, 8 * (4 * b + 4) + 2)
                pe.wait_ge(kt_d, 8 * (4 * b + 4) + 2)
                for t in range(9):
                    last = pe.transpose(PS[:, ACC[t // 4], (t % 4) * P:(t % 4 + 1) * P], SROW[:, t * P:(t + 1) * P], IDENT[:])
                    if t in (3, 7, 8):
                        last.then_inc(s_ptt, 1)
                pe.wait_ge(s_ptc, 3 * b + 3)

        def kt_wait(eng, q, j, hh):
            eng.wait_ge(kt_tr, 16 * q + 4 * j + hh + 1)
            eng.wait_ge(ks_head, 4 * q + hh + 1)
            return KT[hh // 2][:, hh % 2, j, :, :].rearrange("p h n -> p (h n)")

        def kphase_act(act):
            act.wait_ge(s_pc, HEADS)
            act.wait_ge(s_pb, HEADS)
            act.wait_ge(s_kv, 16 * 6)
            act.sem_inc(kt_a, 1)
            act.sem_inc(kt_a, 1)
            for b in range(2):
                with act.Fori(0, 4) as tp:
                    for j in range(4):
                        for hh in (0, 2):
                            dst = kt_wait(act, 4 * b + tp, j, hh)
                            act.activation(dst, PS[:, ACC[hh], :], ACT.Copy).then_inc(kt_a, 1)
                act.wait_ge(s_max, b + 1)
                act.activation(SROW[:, 0:PAST + 32], SROW[:, 0:PAST + 32], ACT.Exp, bias=NMAX, accum_out=ZSUM).then_inc(s_exp, 1)
                for t in range(3):
                    act.wait_ge(s_ptt, 3 * b + t + 1)
                    n = 512 if t < 2 else P
                    act.activation(PT[:, b].rearrange("p t c -> p (t c)")[:, 512 * t:512 * t + n], PS[:, ACC[t], 0:n],
                                   ACT.Copy).then_inc(s_ptc, 1)

        def kphase_dve(dve):
            dve.wait_ge(s_po, HEADS)
            dve.wait_ge(s_kv, 16 * 6)
            link(dve, "dve", dve.memset(QM, 0.0))
            for h in range(HEADS):
                last = dve.tensor_copy(QM[:, :, h, DS * h:DS * h + DS],
                                       Q[:, h, SR0:R].rearrange("p (s i) -> p s i", i=DS))
            last.then_inc(s_qm, 1)
            dve.memset(SROW[:, PAST + 32:], 0.0)
            dve.memset(CMP, 0.0)
            dve.wait_ge(s_pc, HEADS)
            dve.sem_inc(kt_d, 1)
            dve.sem_inc(kt_d, 1)
            dve.sem_inc(ks_free, 1)
            dve.wait_ge(s_own, 1)
            dve.tensor_tensor(OWN, PS[:, M1, 0:64].rearrange("p (b n) -> p b n", b=2), OMASK, ALU.add).then_inc(s_ownc, 1)
            dve.wait_ge(s_ownc, 1)
            for b in range(2):
                with dve.Fori(0, 4) as tp:
                    q = 4 * b + tp
                    for j in range(4):
                        for hh in (1, 3):
                            dst = kt_wait(dve, q, j, hh)
                            dve.tensor_copy(dst, PS[:, ACC[hh], :]).then_inc(kt_d, 1)
                    dve.wait_ge(ks_head, 4 * q + 8)
                    dve.tensor_reduce(GATE[:, bass.ds(tp, 1)], PS[:, M0, 0:BLOCK], AX.X, ALU.add)
                    dve.tensor_tensor(SROW[:, bass.ds(BLOCK * tp, BLOCK)], PS[:, M0, 0:BLOCK],
                                      BIAS[:, bass.ds(BLOCK * tp, BLOCK)], ALU.add).then_inc(ks_free, 1)
                dve.wait_ge(ks_free, 4 * b + 5)
                for n in range(NBLK):
                    if n:
                        dve.tensor_scalar(CMP[:, n, 0:n], GATE[:, 0:n], GATE[:, n:n + 1], None, ALU.is_ge)
                    if n < NBLK - 1:
                        last = dve.tensor_scalar(CMP[:, n, n + 1:], GATE[:, n + 1:], GATE[:, n:n + 1], None, ALU.is_gt)
                link(dve, "dve", dve.tensor_copy(SROW[:, PAST:PAST + 32], OWN[:, b, :]))
                link(dve, "dve", dve.tensor_reduce(PEN, CMP, AX.X, ALU.add))
                link(dve, "dve", dve.tensor_scalar(PEN, PEN, 2.5, NEG, ALU.is_ge, ALU.mult))
                for n in range(NBLK):
                    blk = SROW[:, n * BLOCK:(n + 1) * BLOCK]
                    last = dve.tensor_scalar(blk, blk, PEN[:, n:n + 1], None, ALU.add)
                link(dve, "dve", last)
                dve.tensor_reduce(NMAX, SROW[:, 0:PAST + 32], AX.X, ALU.max, negate=True).then_inc(s_max, 1)
                dve.wait_ge(s_exp, b + 1)
                dve.reciprocal(RZ[:, b:b + 1], ZSUM)
                dve.wait_ge(s_ptt, 3 * b + 3)

        def v_products(pe, quad, v):
            pe.wait_ge(pts_rdy, v + 1)
            for j in range(4):
                pe.wait_ge(x_rdy[j], 32 * quad + 32)
            for t in range(2):
                for half in range(2):
                    for j in range(4):
                        last = pe.matmul(PS[32 * j:32 * j + 32, M2 + half, :], PTS[:, t, 32 * j:32 * j + 32],
                                         XR[:, j, t * 1024 + half * 512:t * 1024 + half * 512 + 512],
                                         start=False, stop=False, skip_group_check=True)
                        if t == 1 and half == 1:
                            last.then_inc(x_used, 1)

        def rest_pe(pe):
            products(pe, P_REST, 0, 0)
            for b in range(2):
                if b == 0:
                    pe.wait_ge(s_vz, 1)
                    pe.wait_ge(s_pf, HEADS)
                else:
                    pe.wait_ge(o_row, 1)
                    o_turn(pe)
                    pe.wait_ge(o_cp, 1)
                for half in range(2):
                    for j in range(4):
                        pe.matmul(PS[32 * j:32 * j + 32, M2 + half, :], PT[:, b, 8, 32 * j:32 * j + 32],
                                  VNEW[:, half * 512:half * 512 + 512], start=True, stop=False, skip_group_check=True)
                if b == 0:
                    with pe.Fori(0, 2) as u:
                        rest_unit(pe, u)
                        products(pe, P_REST + 4 * u + 4, 0, 0)
                else:
                    rest_unit(pe, 2)
                    products(pe, P_REST + 12, 0, 0)
                    rest_unit(pe, 3)
            pe.wait_ge(o_row, 2)
            o_turn(pe)

        def rest_unit(pe, u):
            quad, p = X_REST + 3 * u, P_REST + 4 * u
            ada_sum_block(pe, quad, A_REST + u)
            products(pe, p + 1, 1, 0)
            ada_turn(pe, A_REST + u)
            v_products(pe, quad + 1, 2 * u)
            products(pe, p + 2, 0, 0)
            products(pe, p + 3, 1, 0)
            v_products(pe, quad + 2, 2 * u + 1)

        def o_turn(pe):
            for h in range(HEADS):
                last = pe.transpose(PS[:, M2 + h // 4, (h % 4) * P:(h % 4 + 1) * P], OROW[:, h * P:(h + 1) * P], IDENT[:])
            last.then_inc(o_tr, 1)

        def rest_act(act):
            with act.Fori(0, 4) as u:
                p = P_REST + 4 * u
                split_hi4(act, p)
                split_hi4(act, p + 1)
                ada_copy(act, X_REST + 3 * u, A_REST + u)
                split_hi4(act, p + 2)
                split_hi4(act, p + 3)

        def o_scale(dve, b):
            dve.wait_ge(x_used, 4 * (X_REST + 6 * b + 6))
            dve.tensor_scalar(OROW.rearrange("p (a n) -> p a n", a=2), PS[:, M2:M3 + 1, :], RZ[:, b:b + 1], None,
                              ALU.mult).then_inc(o_row, 1)

        def o_place(dve, b):
            dve.wait_ge(o_tr, b + 1)
            for h in range(HEADS):
                src = PS[:, M2 + h // 4, (h % 4) * P:(h % 4 + 1) * P].rearrange("p (j g q) -> p j g q", j=4, g=HEADS)[:, :, h, :]
                dst = Q[:, h, SR0 + 16 * b:SR0 + 16 * b + 16].rearrange("p (j q) -> p j q", j=4)
                last = dve.tensor_copy(dst, src)
            last.then_inc(o_cp, 1)

        def rest_dve(dve):
            for u in range(4):
                p, n = P_REST + 4 * u, 24 + 8 * u
                split_lo4(dve, p)
                if u:
                    copy_out(dve, p - 1, 1, n - 2)
                if u == 2:
                    o_scale(dve, 0)
                split_lo4(dve, p + 1)
                if u == 2:
                    o_place(dve, 0)
                copy_out(dve, p, 0, n)
                split_lo4(dve, p + 2)
                copy_out(dve, p + 1, 1, n + 2)
                ada_reduce(dve, A_REST + u, 8 + u, 0)
                split_lo4(dve, p + 3)
                copy_out(dve, p + 2, 0, n + 4)
            copy_out(dve, P_OUT0 - 1, 1, 54)
            split_lo4(dve, P_OUT0)
            o_scale(dve, 1)
            o_place(dve, 1)

        def rest_pool(pool):
            pool.wait_ge(s_ptc, 6)
            for v in range(8):
                quad = X_REST + 3 * (v // 2) + 1 + v % 2
                if v:
                    last = quad - 1 if v % 2 else quad - 2
                    pool.wait_ge(x_used, 4 * last + 4)
                pool.tensor_copy(PTS, PT[:, v // 4, 2 * (v % 4):2 * (v % 4) + 2, :]).then_inc(pts_rdy, 1)

        MIXS = A(24 * R + 2048, 256).rearrange("p (g s t) -> p g s t", g=GC, s=NS)
        MIXT = A(16 * R + 2048, 256).rearrange("p (g s t) -> p g s t", g=GC, s=NS)

        def gmlp_pool(pool):
            pool.wait_ge(o_row, 2)
            pool.dma_start(WSROW, a_ws[0].rearrange("g t s -> t g s")).then_inc(g_wld, 16)
            for g in range(GC):
                pool.dma_start(W4[:, 16 * g:16 * g + 16].rearrange("p (t s) -> p t s", s=DS),
                               a_ws[0, g, 0:DS, 0:DS].unsqueeze(0).to_broadcast([P, DS, DS])).then_inc(g_w4, 16)
            pool.wait_ge(g_wld, 16)
            pool.affine_select(out=WSROW, in_=WSROW, compare_op=ALU.is_ge, fill=0.0, base=0,
                               pattern=[[0, GC], [-1, P]], channel_multiplier=1).then_inc(g_ws, 1)
            pool.wait_ge(g_yb, 1)
            pool.dma_start(BSB, a_bs.rearrange("o g t -> o (g t)").to_broadcast([P, GC * P])).then_inc(g_bs, 16)
            pool.wait_ge(g_av, 2)
            pool.dma_start(av_v, AVROW).then_inc(g_avst, 16)

        def gmlp_act(act):
            split_hi4(act, P_OUT0)
            act.wait_ge(acc_free, P_OUT0)
            act.activation(VA, VA, ACT.Gelu_apprx_tanh).then_inc(g_act, 1)
            act.activation(U, U, ACT.Gelu_apprx_tanh).then_inc(g_act, 1)
            act.activation(ZB, ZB, ACT.Silu).then_inc(g_act, 1)
            act.activation(ZA, ZA, ACT.Silu).then_inc(g_act, 1)
            act.wait_ge(g_ln, 1)
            squares(act, VA, GC, KC)
            root(act, 2)
            act.wait_ge(g_yb, 1)
            act.wait_ge(w_used, 4 * P_OUT0)
            for k in range(GC):
                act.activation(HH[:, GC + k, :], Q[:, k, :], ACT.Copy).then_inc(s_hh, 1)
            for x in range(2):
                act.wait_ge(g_vt, 2 * x + 1)
                act.activation(VAROW[:, x, 0:512], PS[:, ACC[2 * x], :], ACT.Copy).then_inc(g_vca, 1)
            act.wait_ge(g_vt, 5)
            act.activation(AVROW[:, 0:512], PS[0:NS * DS, M2, :], ACT.Copy).then_inc(g_av, 1)
            for k in range(GC):
                act.wait_ge(g_ya, 1)
                act.activation(HH[:, k, :], VA[:, k, :], ACT.Copy).then_inc(s_hh, 1)

        def gmlp_pe(pe):
            pe.wait_ge(g_act, 1)
            for k in range(GC):
                last = pe.matmul(PS[:, M0, 0:R], ONES[:], VA[:, k, :], start=k == 0, stop=k == GC - 1)
            last.then_inc(g_mean, 1)
            sum_squares(pe, GC, KC, M1)
            pe.wait_ge(g_ws, 1)
            pe.wait_ge(o_cp, 2)
            for g in range(GC):
                last = pe.transpose(PS[:, M2 + g // 4, (g % 4) * P:(g % 4 + 1) * P], WSROW[:, g, :], IDENT[:])
            last.then_inc(g_wst, 1)
            pe.wait_ge(g_vn, GC)
            for c in range(2):
                for half in range(2):
                    for x in range(4):
                        last = pe.transpose(PS[:, ACC[2 * c + half], x * P:(x + 1) * P],
                                            VA[:, 4 * half + x, c * P:(c + 1) * P], IDENT[:])
                    last.then_inc(g_vt, 1)
            pe.wait_ge(g_wsc, 1)
            for g in range(GC):
                last = pe.transpose(PS[0:NS * DS, M2 + g // 4, (g % 4) * P:(g % 4 + 1) * P], VA[:, g, SR0:R], IDENT[:])
            last.then_inc(g_vt, 1)
            pe.wait_ge(g_vca, 2)
            pe.wait_ge(g_vcd, 2)
            for g in range(GC):
                if g >= 4:
                    pe.wait_ge(g_mr, g - 3)
                for c in range(2):
                    last = pe.matmul(PS[:, ACC[g % 4], c * P:(c + 1) * P], VAROW[:, c, g * P:(g + 1) * P],
                                     WST[:, g, :], start=True, stop=True)
                last.then_inc(g_mix, 1)

        def gmlp_dve(dve):
            dve.wait_ge(g_mean, 1)
            link(dve, "dve", dve.tensor_scalar(RB, PS[:, M0, 0:R], 1.0 / DA, None, ALU.mult))
            dve.tensor_tensor(VA, VA, bc(RB.unsqueeze(1), [P, GC, R]), ALU.subtract).then_inc(g_ln, 1)
            dve.wait_ge(g_act, 3)
            dve.wait_ge(o_cp, 2)
            dve.tensor_tensor(Q, Q, ZB, ALU.mult).then_inc(g_yb, 1)
            variance_inverse(dve, KC + GC, M1, DA, 2)
            for k in range(GC):
                lo_part(dve, Q, k, GC + k, KC + k)
            dve.wait_ge(s_root, 2)
            link(dve, "dve", dve.tensor_tensor(VA, VA, bc(RB.unsqueeze(1), [P, GC, R]), ALU.mult))
            for k in range(GC):
                dve.tensor_scalar(VA[:, k, :], VA[:, k, :], V_ALNG[:, k:k + 1], V_ALNB[:, k:k + 1], ALU.mult, ALU.add).then_inc(g_vn, 1)
            dve.wait_ge(g_wst, 1)
            dve.tensor_copy(WST, PS[:, M2:M3 + 1, :].rearrange("p a (g t) -> p (a g) t", t=P)).then_inc(g_wsc, 1)
            for x in range(2):
                dve.wait_ge(g_vt, 2 * x + 2)
                dve.tensor_copy(VAROW[:, x, 512:1024], PS[:, ACC[2 * x + 1], :]).then_inc(g_vcd, 1)
            dve.wait_ge(g_vt, 5)
            dve.tensor_copy(AVROW[:, 512:1024], PS[0:NS * DS, M3, :]).then_inc(g_av, 1)
            dve.wait_ge(g_w4, 16 * GC)
            dve.wait_ge(g_bs, 16)
            dve.wait_ge(g_vn, GC)
            vs = part(VA[:, :, SR0:R])
            for s in range(DS):
                n = DS - s
                w = W4.rearrange("p (g t s) -> p g t s", g=GC, t=DS)[:, :, s:, s].unsqueeze(2)
                dst = MIXS if s == 0 else MIXT
                link(dve, "dve", dve.tensor_tensor(dst[:, :, :, s:], bc(vs[:, :, :, s:s + 1], [P, GC, NS, n]),
                                                   bc(w, [P, GC, NS, n]), ALU.mult))
                if s:
                    link(dve, "dve", dve.tensor_tensor(MIXS[:, :, :, s:], MIXS[:, :, :, s:], MIXT[:, :, :, s:], ALU.add))
            dve.tensor_tensor(vs, MIXS, bc(BSB[:, :, 0:DS].unsqueeze(2), [P, GC, NS, DS]), ALU.add)
            for g in range(GC):
                dve.wait_ge(g_mix, g + 1)
                last = dve.tensor_tensor(VA[:, g, 0:SEQ].rearrange("p (c t) -> p c t", c=2),
                                         PS[:, ACC[g % 4], 0:SEQ].rearrange("p (c t) -> p c t", c=2),
                                         bc(BSB[:, g, :].unsqueeze(1), [P, 2, P]), ALU.add)
                last.then_inc(g_mr, 1)
            dve.wait_ge(g_mr, GC)
            dve.wait_ge(g_act, 4)
            link(dve, "dve", dve.tensor_tensor(VA, VA, U, ALU.mult))
            dve.tensor_tensor(VA, VA, ZA, ALU.mult).then_inc(g_ya, 1)
            for k in range(GC):
                lo_part(dve, VA, k, k, KC + GC + k)

        def out0_pe(pe):
            pe.wait_ge(g_mr, GC)
            with pe.Fori(0, 2) as i:
                p = P_OUT0 + 4 * i
                ada_sum_block(pe, X_OUT0 + i, A_OUT0 + i)
                products(pe, p, 0, KC, turn=2)
                products(pe, p + 1, 1, KC, turn=2)
                ada_turn(pe, A_OUT0 + i)
                products(pe, p + 2, 0, KC, turn=2)
                products(pe, p + 3, 1, KC, turn=2)

        def out0_act(act):
            for i in range(2):
                p = P_OUT0 + 4 * i
                if i:
                    split_hi4(act, p)
                ada_copy(act, X_OUT0 + i, A_OUT0 + i)
                split_hi4(act, p + 1)
                split_hi4(act, p + 2)
                split_hi4(act, p + 3)

        def out0_dve(dve):
            for i in range(4):
                p = P_OUT0 + 2 * i
                if i:
                    split_lo4(dve, p)
                    add_gated(dve, p - 1, 1, 4 * i - 2, 2 * i - 1)
                if i in (1, 3):
                    ada_reduce(dve, A_OUT0 + i // 2, 6 + i // 2, 1)
                split_lo4(dve, p + 1)
                add_gated(dve, p, 0, 4 * i, 2 * i if i else None)
            add_gated(dve, P_AB - 1, 1, 14, 7)
            scale_times_gain(dve, 1)

        def state_pool(pool):
            pool.wait_ge(s_hl, 2 * KC)
            pool.wait_ge(g_avst, 16)
            pool.wait_ge(s_kv, 16 * 6)
            pool.memset(GLU[:, :, 0:HALO], 0.0).then_inc(s_zero, 1)
            for t in range(2):
                pool.dma_start(STROW[t], state_conv[0, 4 * t:4 * t + 4].rearrange("s w d -> (s w) d")).then_inc(st_ld, 16)
            store(pool, conv_sample[0, :, 0:HALO - DS, :], state_conv[0, :, DS:HALO, :])

        def state_pe(pe):
            pe.wait_ge(st_ld, 32)
            for f in range(8):
                t, g = f // 4, f % 4
                bank = (M2, M3)[f % 2]
                if f >= 2:
                    pe.wait_ge(st_cp, f - 1)
                for x in range(4):
                    last = pe.transpose(PS[:, bank, x * 120:(x + 1) * 120], STROW[t][:, (4 * g + x) * P:(4 * g + x + 1) * P],
                                        IDENT[0:120, 0:120])
                last.then_inc(st_tr, 1)

        def state_act(act):
            for f in range(8):
                t, g = f // 4, f % 4
                act.wait_ge(st_tr, f + 1)
                dst = GLU[:, 4 * g:4 * g + 4, SEQ + HALO:GP].rearrange("p c (s o) -> p c s o", o=EXPOS)
                act.activation(dst[:, :, 4 * t:4 * t + 4, 0:HALO],
                               PS[:, (M2, M3)[f % 2], 0:480].rearrange("p (c s w) -> p c s w", c=4, w=HALO),
                               ACT.Copy).then_inc(st_cp, 1)

        def norm1_act(act):
            split_hi4(act, P_AB)
            act.wait_ge(s_res, 8)
            act.wait_ge(ada_tr, A_AB)
            squares(act, XT, KC, KC + GC)
            act.wait_ge(s_sqmm, 2 * KC + GC)
            root(act, 3)
            modulate(act, KC, 4 * P_AB)

        def norm1_dve(dve):
            variance_inverse(dve, 2 * KC + GC, M3, D, 3)
            dve.wait_ge(st_tr, 8)
            normalise(dve, 3, 2 * KC)

        def glu_in(dve, d):
            m = 2 * d
            dve.wait_ge(w_used, 4 * (P_AB + 2 * d) + 4)
            dve.tensor_copy(GLU[:, bass.ds(m, 2), HALO:HALO + SEQ], PS[:, 0:2, 0:SEQ])
            dst = GLU[:, bass.ds(m, 2), SEQ + HALO:GP].rearrange("p c (s o) -> p c s o", o=EXPOS)[:, :, :, HALO:EXPOS]
            dve.tensor_copy(dst, part(PS[:, 0:2, SR0:R])).then_inc(acc_free, 1)

        def glu_gate(dve, d):
            m = 2 * d
            dve.wait_ge(acc_free, P_AB + 2 * d + 2)
            sig = Y[:, bass.ds(m, 2), :]
            g = GLU[:, bass.ds(m, 2), HALO:HALO + SEQ]
            dve.tensor_tensor(g, g, sig[:, :, 0:SEQ], ALU.mult)
            g = GLU[:, bass.ds(m, 2), SEQ + HALO:GP].rearrange("p c (s o) -> p c s o", o=EXPOS)[:, :, :, HALO:EXPOS]
            dve.tensor_tensor(g, g, part(sig[:, :, SR0:R]), ALU.mult).then_inc(s_glu, 1)

        def sigmoid_b(act, d):
            act.wait_ge(w_used, 4 * (P_AB + 2 * d + 1) + 4)
            act.wait_ge(acc_free, P_AB + 2 * d + 1)
            act.activation(Y[:, bass.ds(2 * d, 2), :], PS[:, 2:4, 0:R], ACT.Sigmoid).then_inc(acc_free, 1)

        def spread(act, m, piece, first=False):
            lo, hi = (0, 17) if piece == 0 else (17, EXPOS)
            if not first:
                act.wait_ge(s_tap, TAPN * (m - 1) + (17 if piece == 0 else TAPN))
            g = GLU[:, bass.ds(m, 1), :].rearrange("p c n -> p (c n)")
            gp = g[:, lo:]
            src = bass.AP(tensor=gp.tensor, offset=gp.offset, ap=[gp.ap[0], [1, hi - lo], [4, 64]])
            act.activation(EX[:, lo:hi, 0:64], src, ACT.Copy)
            srcs = g[:, SEQ + HALO:GP].rearrange("p (s o) -> p o s", o=EXPOS)[:, lo:hi, :]
            act.activation(EX[:, lo:hi, 64:TAPROWS], srcs, ACT.Copy).then_inc(s_ex, 1)

        TAPN = CW + 1

        def taps(dve, m, w0, w1):
            y = Y[:, bass.ds(m, 1), :].rearrange("p c r -> p (c r)")
            n0 = TAPN * m
            for w in range(w0, w1):
                if w == 0:
                    dve.wait_ge(s_ex, 2 * m + 1)
                if w == 14:
                    dve.wait_ge(s_ex, 2 * m + 2)
                src = EX[:, w:w + DS, :].rearrange("p o l -> p (o l)")
                tap = CWT[:, bass.ds(m, 1), w:w + 1].rearrange("p a b -> p (a b)")
                dst = y if w % 2 == 0 else RB
                if w >= 2:
                    dve.wait_ge(s_tap, n0 + w - 1)
                if w == 0:
                    ins = dve.tensor_scalar(dst, src, tap, V_CB[:, bass.ds(m, 1)], ALU.mult, ALU.add)
                elif w == 1:
                    ins = dve.tensor_scalar(dst, src, tap, None, ALU.mult)
                else:
                    ins = dve.scalar_tensor_tensor(dst, src, tap, dst, ALU.mult, ALU.add)
                ins.then_inc(s_tap, 1)
            if w1 == CW:
                dve.wait_ge(s_tap, n0 + CW)
                dve.tensor_tensor(y, y, RB, ALU.add).then_inc(s_tap, 1)
                dve.wait_ge(s_tap, n0 + TAPN)

        def taps_part(dve, m, s):
            if s == 0:
                taps(dve, m, 0, 23)
            elif s == 1:
                taps(dve, m, 23, CW)
                taps(dve, m + 1, 0, 15)
            elif s == 2:
                taps(dve, m + 1, 15, CW)
                taps(dve, m + 2, 0, 7)
            else:
                taps(dve, m + 2, 7, CW)

        def spread_part(act, m, p, s, last=False):
            split_hi(act, p, 0)
            if s == 0:
                spread(act, m, 1)
            elif s == 2:
                spread(act, m + 2, 0)
            split_hi(act, p, 1)
            if s == 1:
                spread(act, m + 1, 1)
            split_hi(act, p, 2)
            split_hi(act, p, 3)
            if s == 0:
                spread(act, m + 1, 0)
            elif s == 2:
                spread(act, m + 2, 1)
            elif s == 3 and not last:
                spread(act, m + 3, 0)

        def ab_pe(pe):
            with pe.Fori(0, 4) as i:
                p = P_AB + 4 * i
                products(pe, p, 0, 2 * KC)
                products(pe, p + 1, 1, 2 * KC)
                ada_sum_block(pe, X_AB + i, A_AB + i)
                products(pe, p + 2, 0, 2 * KC)
                ada_turn(pe, A_AB + i)
                products(pe, p + 3, 1, 2 * KC)

        def ab_turn_act(act, i, m):
            p = P_AB + 4 * i + 2
            for s in range(4):
                if s % 2:
                    sigmoid_b(act, 2 * i + s // 2)
                if s == 1:
                    ada_copy(act, X_AB + i, A_AB + i)
                if m is not None:
                    spread_part(act, m, p + s, s)
                else:
                    split_hi4(act, p + s)
                    if s == 1:
                        act.wait_ge(s_glu, 1)
                        act.wait_ge(s_zero, 1)
                        spread(act, 0, 0, first=True)
                        spread(act, 0, 1, first=True)
                    if s == 3:
                        spread(act, 1, 0)

        def ab_act(act):
            split_hi4(act, P_AB + 1)
            ab_turn_act(act, 0, None)
            with act.Fori(1, 4) as i:
                ab_turn_act(act, i, 3 * i - 2)

        def ab_turn_dve(dve, i, m):
            for s in range(4):
                if s % 2 == 0:
                    glu_in(dve, 2 * i + s // 2)
                else:
                    glu_gate(dve, 2 * i + s // 2)
                if s == 3:
                    ada_reduce(dve, A_AB + i, 8 + i, 1)
                if m is not None:
                    taps_part(dve, m, s)
                elif s == 2:
                    taps(dve, 0, 0, 16)
                elif s == 3:
                    taps(dve, 0, 16, CW)

        def ab_dve(dve):
            ab_turn_dve(dve, 0, None)
            with dve.Fori(1, 4) as i:
                ab_turn_dve(dve, i, 3 * i - 2)

        def z_pe(pe):
            with pe.Fori(0, 4) as i:
                products(pe, P_Z + 2 * i, 0, 2 * KC)
                products(pe, P_Z + 2 * i + 1, 1, 2 * KC)

        def z_act(act):
            for i in range(2):
                for s in range(4):
                    p = P_Z + 4 * i + s
                    act.wait_ge(w_used, 4 * p + 4)
                    n = 2 * (p - P_Z)
                    act.activation(Z[:, n:n + 2, :], PS[:, 2 * (s % 2):2 * (s % 2) + 2, 0:R], ACT.Silu).then_inc(acc_free, 1)
                    if i == 0 or s < 3:
                        spread_part(act, 10 + 3 * i, p + 2, s)

        def z_dve(dve):
            for i in range(2):
                for s in range(4):
                    taps_part(dve, 10 + 3 * i, s)

        YN = chunks(0, KC)
        CL = A(15072, KC * 62).rearrange("p (c n) -> p c n", n=62)
        CPROW = A(KC * R, D, 62)

        def cln_pool(pool):
            pool.wait_ge(s_tap, TAPN * KC)
            pool.tensor_copy(CL[:, :, 0:HALO], GLU[:, :, SEQ:SEQ + HALO])
            src = GLU[:, :, SEQ + HALO:GP].rearrange("p c (s o) -> p c s o", o=EXPOS)[:, :, :, HALO:EXPOS]
            pool.tensor_copy(CL[:, :, HALO:62].rearrange("p c (s i) -> p c s i", i=DS), src).then_inc(cl_rdy, 1)

        def cln_pe(pe):
            for k in range(KC):
                pe.wait_ge(s_tap, TAPN * (k + 1))
                last = pe.matmul(PS[:, M0, 0:R], ONES[:], Y[:, k, :], start=k == 0, stop=k == KC - 1)
            last.then_inc(ln_mean, 1)
            pe.wait_ge(cl_rdy, 1)
            pe.wait_ge(acc_free, P_OUT1)
            for k in range(KC):
                last = pe.transpose(PS[0:62, ACC[k // 4], (k % 4) * P:(k % 4 + 1) * P], CL[:, k, :], IDENT[:])
            last.then_inc(cp_tr, 1)
            sum_squares(pe, KC, 2 * KC + GC, M1)
            pe.wait_ge(cp_cp, 1)

        def cln_dve(dve):
            dve.wait_ge(ln_mean, 1)
            link(dve, "dve", dve.tensor_scalar(RB, PS[:, M0, 0:R], 1.0 / D, None, ALU.mult))
            for k in range(KC):
                dve.tensor_tensor(Y[:, k, :], Y[:, k, :], RB, ALU.subtract).then_inc(ln_y, 1)
            variance_inverse(dve, 3 * KC + GC, M1, D, 4)
            dve.wait_ge(s_root, 4)
            dve.wait_ge(cl_rdy, 1)
            dve.wait_ge(cp_tr, 1)
            for k in range(KC + 4):
                if k < KC:
                    dve.tensor_tensor(Y[:, k, :], Y[:, k, :], RB, ALU.mult).then_inc(ln_r, 1)
                if 2 <= k < KC + 2:
                    dve.wait_ge(ln_s, k - 1)
                    dve.tensor_tensor(YN[:, k - 2, :].rearrange("p (l i) -> p l i", i=DS),
                                      Y[:, k - 2, :].rearrange("p (i l) -> p l i", i=DS),
                                      Z[:, k - 2, :].rearrange("p (l i) -> p l i", i=DS), ALU.mult).then_inc(ln_z, 1)
                if k >= 4:
                    lo_part(dve, YN, k - 4, k - 4, 3 * KC + k - 4)

        def cln_act(act):
            base = 2 * KC + GC
            for k in range(KC):
                act.wait_ge(ln_y, k + 1)
                if k >= 2:
                    act.wait_ge(s_sqmm, base + k - 1)
                act.activation(SQ[k % 2], Y[:, k, :], ACT.Square).then_inc(s_sq, 1)
            root(act, 4)
            act.wait_ge(w_used, 4 * P_OUT1)
            for k in range(KC + 2):
                if k < KC:
                    act.wait_ge(ln_r, k + 1)
                    act.activation(Y[:, k, :], Y[:, k, :], ACT.Silu, bias=V_CLNB[:, k:k + 1], scale=V_CLNG[:, k:k + 1]).then_inc(ln_s, 1)
                if k >= 2:
                    act.wait_ge(ln_z, k - 1)
                    act.activation(HH[:, k - 2, :], YN[:, k - 2, :], ACT.Copy).then_inc(s_hh, 1)
            act.wait_ge(cp_tr, 1)
            act.activation(CPROW.rearrange("p (a n) -> p a n", a=4), PS[0:62, 0:4, :], ACT.Copy).then_inc(cp_cp, 1)

        def out1_pe(pe):
            with pe.Fori(0, 4) as i:
                products(pe, P_OUT1 + 2 * i, 0, 3 * KC)
                products(pe, P_OUT1 + 2 * i + 1, 1, 3 * KC)
            sum_squares(pe, KC, 3 * KC + GC, M0)
            for f in range(12):
                rt, g = f // 4, f % 4
                rows = P if rt < 2 else NS * DS
                pe.wait_ge(f_row, 4 * g + 4)
                if f >= 8:
                    pe.wait_ge((f_cpa, f_cpd)[f % 2], (f - 8) // 2 + 1)
                for x in range(4):
                    bank = (ACC + [M1, M2, M3, M0])[f % 8]
                    last = pe.transpose(PS[0:rows, bank, x * P:(x + 1) * P], YF[:, 4 * g + x, rt * P:rt * P + rows], IDENT[:])
                last.then_inc(f_tr, 1)

        YF = chunks(0, KC)

        def out1_act(act):
            with act.Fori(1, 8) as i:
                split_hi4(act, P_OUT1 + i)
            act.wait_ge(s_res, 16)
            squares(act, XT, KC, 3 * KC + GC)
            root(act, 5)
            for f in range(0, 12, 2):
                final_copy(nc.scalar, act, f).then_inc(f_cpa, 1)

        def final_copy(eng, q, f):
            rt, g = f // 4, f % 4
            rows = P if rt < 2 else NS * DS
            q.wait_ge(f_tr, f + 1)
            dst, src = YROW[rt][:, g * 512:(g + 1) * 512], PS[0:rows, (ACC + [M1, M2, M3, M0])[f % 8], :]
            return eng.activation(dst, src, ACT.Copy) if eng is nc.scalar else eng.tensor_copy(dst, src)

        def out1_dve(dve):
            with dve.Fori(0, 4) as i:
                add_gated(dve, P_OUT1 + 2 * i, 0, 4 * i, 8 + 2 * i)
                add_gated(dve, P_OUT1 + 2 * i + 1, 1, 4 * i + 2, 9 + 2 * i)
            variance_inverse(dve, 4 * KC + GC, M0, D, 5)
            dve.wait_ge(s_root, 5)
            for k in range(KC):
                dve.scalar_tensor_tensor(YF[:, k, :], XT[:, k, :], V_FIN[:, k:k + 1], RB, ALU.mult, ALU.mult).then_inc(f_row, 1)
            for f in range(1, 12, 2):
                final_copy(nc.vector, dve, f).then_inc(f_cpd, 1)

        def out1_pool(pool):
            with pool.Fori(1, 8) as i:
                split_lo4(pool, P_OUT1 + i)
            pool.wait_ge(cp_cp, 1)
            store(pool, conv_prompt[0, 0], CPROW[0:HALO])
            for s in range(NS):
                store(pool, conv_sample[0, s, HALO - DS:HALO, :], CPROW[HALO + DS * s:HALO + DS * s + DS])

        def rest_col(n):
            return 256 * (24 + n if n < 4 else n - 4)

        @block.sync
        def _(sp):
            load_ada(sp, 0, 0, 0, first=True)
            load_pair(sp, 0, win_v, 12 * 256, first=True)
            with sp.Fori(1, 8) as a:
                load_ada(sp, a, 0, 512 * a)
            load_ada(sp, X_QKV, 1, 0)
            load_pair(sp, 1, win_v, 13 * 256)
            load_ada(sp, X_QKV + 1, 1, 512)
            with sp.Fori(1, 5) as i:
                load_pair(sp, 2 * i, win_v, (12 + 2 * i) * 256)
                load_pair(sp, 2 * i + 1, win_v, (13 + 2 * i) * 256)
                load_ada(sp, X_QKV + 1 + i, 1, 512 * (i + 1))
            load_pair(sp, 10, win_v, 22 * 256)
            load_pair(sp, 11, win_v, 23 * 256)
            sp.wait_ge(s_ptab, 16)
            for b in range(2):
                with sp.Fori(0, 4) as tp:
                    load_pages(sp, X_K + 4 * b + tp, b, tp, kc_v)
            load_ada(sp, X_REST, 0, 512 * 8)
            sp.wait_ge(ks_head, 4 + 4 * 8)
            load_pair(sp, P_REST, win_v, rest_col(0))
            load_pair(sp, P_REST + 1, win_v, rest_col(1))
            for u in range(4):
                p = P_REST + 4 * u
                load_pair(sp, p + 2, win_v, rest_col(4 * u + 2))
                load_pages(sp, X_REST + 3 * u + 1, u // 2, 2 * (u % 2), vc_v)
                load_pair(sp, p + 3, win_v, rest_col(4 * u + 3))
                load_pages(sp, X_REST + 3 * u + 2, u // 2, 2 * (u % 2) + 1, vc_v)
                if u < 3:
                    load_pair(sp, p + 4, win_v, rest_col(4 * u + 4))
                    load_pair(sp, p + 5, win_v, rest_col(4 * u + 5))
                    load_ada(sp, X_REST + 3 * u + 3, 0, 512 * (9 + u))
            load_ada(sp, X_OUT0, 1, 512 * 6)
            for i in range(8):
                load_pair(sp, P_OUT0 + i, wout_v, 256 * i, turn=2)
                if i in (1, 5):
                    load_ada(sp, X_OUT0 + 1 + i // 4, 1, 512 * (7 + i // 4))
            for i in range(4):
                for s in range(4):
                    d = 2 * i + s // 2
                    load_pair(sp, P_AB + 4 * i + s, cin_v, 256 * d + D * (s % 2))
                if i < 3:
                    load_ada(sp, X_AB + i + 1, 1, 512 * (9 + i))
            with sp.Fori(0, 8) as i:
                load_pair(sp, P_Z + i, cin_v, 2 * D + 256 * i)
            with sp.Fori(0, 8) as i:
                load_pair(sp, P_OUT1 + i, cout_v, 256 * i)
            sp.wait_ge(f_cpa, 2)
            sp.wait_ge(f_cpd, 2)
            sp.dma_start(yp_v[0:P], YROW[0]).then_inc(s_fin, 16)
            sp.wait_ge(f_cpa, 4)
            sp.wait_ge(f_cpd, 4)
            sp.dma_start(yp_v[P:2 * P], YROW[1]).then_inc(s_fin, 16)
            sp.wait_ge(f_cpa, 6)
            sp.wait_ge(f_cpd, 6)
            sp.dma_start(ys_v, YROW[2]).then_inc(s_fin, 16)
            sp.wait_ge(s_fin, 48)

        @block.tensor
        def _(pe):
            start_pe(pe)
            qkv_pe(pe)
            rows_pe(pe)
            prompt_pe(pe)
            kphase_pe(pe)
            rest_pe(pe)
            gmlp_pe(pe)
            out0_pe(pe)
            state_pe(pe)
            sum_squares(pe, KC, KC + GC, M3)
            ab_pe(pe)
            z_pe(pe)
            cln_pe(pe)
            out1_pe(pe)

        @block.scalar
        def _(act):
            start_act(act)
            qkv_act(act)
            rows_act(act)
            prompt_act(act)
            kphase_act(act)
            rest_act(act)
            gmlp_act(act)
            out0_act(act)
            state_act(act)
            norm1_act(act)
            ab_act(act)
            z_act(act)
            cln_act(act)
            out1_act(act)

        @block.vector
        def _(dve):
            start_dve(dve)
            qkv_dve(dve)
            rows_dve(dve)
            prompt_dve(dve)
            kphase_dve(dve)
            rest_dve(dve)
            gmlp_dve(dve)
            out0_dve(dve)
            norm1_dve(dve)
            ab_dve(dve)
            z_dve(dve)
            cln_dve(dve)
            out1_dve(dve)

        @block.gpsimd
        def _(pool):
            start_pool(pool)
            rows_pool(pool)
            rest_pool(pool)
            gmlp_pool(pool)
            state_pool(pool)
            with pool.Fori(0, PAIRS_AB + PAIRS_Z + 1) as i:
                split_lo4(pool, P_AB + i)
            cln_pool(pool)
            out1_pool(pool)
            pool.wait_ge(s_kv, 16 * 6)
            pool.wait_ge(g_avst, 16)
            pool.wait_ge(s_out, 16 * OUTS[0])


def kernel(**inputs):
    import numpy as np
    import concourse.bacc as bacc
    from concourse.bass_utils import run_bass_kernel_spmd

    nc = bacc.Bacc("TRN2", target_bir_lowering=False, num_devices=1)
    names = ["x_prompt", "x_sample", "cache_b_k", "cache_b_v", "state_c_conv", "page_table", "c_prompt", "c_sample",
             "ada_w", "ada_b", "norm_g", "ab_w_in", "a_ln_g", "a_ln_b", "a_ws", "a_bs", "ab_w_out",
             "c_w_in", "c_conv_w", "c_conv_b", "c_ln_g", "c_ln_b", "c_w_out", "final_norm_g"]
    outs = [(1, SEQ, D), (NS, DS, D), (1, 1, SEQ, HEADS, HD), (1, 1, SEQ, HEADS, HD), (1, NS, DS, HEADS, HD),
            (1, NS, DS, HEADS, HD), (1, NS, DS, DA), (1, 1, HALO, D), (1, NS, HALO, D)]
    arrays, args = {}, []
    for name in names:
        a = np.ascontiguousarray(inputs[name])
        arrays["in_" + name] = a
        args.append(nc.dram_tensor("in_" + name, a.shape, mybir.dt.from_np(a.dtype), kind="ExternalInput").ap())
    for i, shape in enumerate(outs):
        args.append(nc.dram_tensor(f"out_{i}", shape, F32, kind="ExternalOutput").ap())
    trunk(nc, *args)
    r = run_bass_kernel_spmd(nc, [arrays], core_ids=[0])
    return tuple(r.results[0][f"out_{i}"] for i in range(len(outs)))
```
